# Optimizing a Trainium2 kernel written in Bass

```python
import math
import jax, jax.numpy as jnp
from jax import lax
import numpy as np

D_MODEL = 1024
BATCH = 1
SEQ = 256
DEPTH = 2

N_SELF = DEPTH // 2
N_CROSS = DEPTH - N_SELF
N_DENSE = (DEPTH + 1) // 2
N_MOE = DEPTH // 2
CONV_WIDTH = 3
N_HEADS = 16
HEAD_DIM = D_MODEL // N_HEADS
BLOCK_Q = 128
D_FF = 2816
D_FF_EXPERT = 2816
N_EXPERTS = 8
TOP_K = 2
RMS_EPS = 1e-6

kernel_name = "yoco_shortconv_stickbreaking_moe"

def rms_norm(x, g):
    xf = x.astype(jnp.float32)
    y = xf * lax.rsqrt(jnp.mean(xf * xf, axis=-1, keepdims=True) + RMS_EPS)
    return (y * g.astype(jnp.float32)).astype(x.dtype)

def swiglu(h, w_gu, w_down):
    gate, up = jnp.split(h @ w_gu, 2, axis=-1)
    return (jax.nn.silu(gate) * up) @ w_down

def short_conv_mixer(h, w_in, conv_w, w_out):
    c_gate, val, b_gate = jnp.split(h @ w_in, 3, axis=-1)
    u = c_gate * val
    conv = lax.conv_general_dilated(
        u, conv_w[:, None, :].astype(u.dtype), window_strides=(1,),
        padding=[(CONV_WIDTH - 1, 0)], dimension_numbers=('NWC', 'WIO', 'NWC'),
        feature_group_count=D_MODEL)
    return (b_gate * conv) @ w_out

def stick_breaking_attention(q, k, v):
    seq = q.shape[1]
    scale = 1.0 / math.sqrt(HEAD_DIM)
    outs = []
    for blk in range(seq // BLOCK_Q):
        t0 = blk * BLOCK_Q
        t1 = t0 + BLOCK_Q
        qb = q[:, t0:t1].astype(jnp.float32)
        kb = k[:, :t1].astype(jnp.float32)
        vb = v[:, :t1]
        z = jnp.einsum('bqhd,bshd->bhqs', qb, kb) * scale
        t_idx = t0 + jnp.arange(BLOCK_Q)[:, None]
        s_idx = jnp.arange(t1)[None, :]
        causal = s_idx < t_idx
        log_1m_beta = jnp.where(causal, jax.nn.log_sigmoid(-z), 0.0)
        suffix = lax.cumsum(log_1m_beta, axis=3, reverse=True) - log_1m_beta
        attn = jnp.where(causal, jnp.exp(jax.nn.log_sigmoid(z) + suffix), 0.0)
        outs.append(jnp.einsum('bhqs,bshd->bqhd', attn.astype(vb.dtype), vb))
    return jnp.concatenate(outs, axis=1)

def moe_swiglu(h, w_router, w_gu, w_down):
    logits = (h @ w_router).astype(jnp.float32)
    top_val, top_idx = lax.top_k(logits, TOP_K)
    top_w = jax.nn.softmax(top_val, axis=-1)
    gates = jnp.sum(jax.nn.one_hot(top_idx, N_EXPERTS, dtype=jnp.float32) * top_w[..., None], axis=1)
    y = jnp.zeros_like(h)
    for e in range(N_EXPERTS):
        y = y + gates[:, e:e + 1].astype(h.dtype) * swiglu(h, w_gu[e], w_down[e])
    return y

def setup_inputs(seed: int = 0) -> dict:
    key = jax.random.key(seed)
    ks = jax.random.split(key, 16)
    f32 = jnp.float32
    d = D_MODEL

    def nrm(k, shape, fan_in):
        return jax.random.normal(k, shape, f32) * (fan_in ** -0.5)

    def gain(k, shape):
        return 1.0 + 0.02 * jax.random.normal(k, shape, f32)

    return {
        "x": jax.random.normal(ks[0], (BATCH, SEQ, d), f32),
        "g_mix": gain(ks[1], (DEPTH, d)),
        "g_ffn": gain(ks[2], (DEPTH, d)),
        "g_final": gain(ks[3], (d,)),
        "a_w_in": nrm(ks[4], (N_SELF, d, 3 * d), d),
        "a_conv_w": nrm(ks[5], (N_SELF, CONV_WIDTH, d), CONV_WIDTH),
        "a_w_out": nrm(ks[6], (N_SELF, d, d), d),
        "g_kv": gain(ks[7], (d,)),
        "w_kv": nrm(ks[8], (d, 2 * d), d),
        "b_w_q": nrm(ks[9], (N_CROSS, d, d), d),
        "b_w_o": nrm(ks[10], (N_CROSS, d, d), d),
        "ffn_w_gu": nrm(ks[11], (N_DENSE, d, 2 * D_FF), d),
        "ffn_w_down": nrm(ks[12], (N_DENSE, D_FF, d), D_FF),
        "moe_w_router": nrm(ks[13], (N_MOE, d, N_EXPERTS), d),
        "moe_w_gu": nrm(ks[14], (N_MOE, N_EXPERTS, d, 2 * D_FF_EXPERT), d),
        "moe_w_down": nrm(ks[15], (N_MOE, N_EXPERTS, D_FF_EXPERT, d), D_FF_EXPERT),
    }

def reference(x, g_mix, g_ffn, g_final, a_w_in, a_conv_w, a_w_out, g_kv, w_kv,
              b_w_q, b_w_o, ffn_w_gu, ffn_w_down, moe_w_router, moe_w_gu, moe_w_down):
    bsz, seq, d = x.shape
    k_shared = None
    v_shared = None
    for i in range(DEPTH):
        if i < N_SELF:
            h = rms_norm(x, g_mix[i])
            x = x + short_conv_mixer(h, a_w_in[i], a_conv_w[i], a_w_out[i])
        else:
            if i == N_SELF:
                kv = rms_norm(x, g_kv) @ w_kv
                k_shared, v_shared = jnp.split(kv, 2, axis=-1)
                k_shared = k_shared.reshape(bsz, seq, N_HEADS, HEAD_DIM)
                v_shared = v_shared.reshape(bsz, seq, N_HEADS, HEAD_DIM)
            j = i - N_SELF
            h = rms_norm(x, g_mix[i])
            q = (h @ b_w_q[j]).reshape(bsz, seq, N_HEADS, HEAD_DIM)
            o = stick_breaking_attention(q, k_shared, v_shared).reshape(bsz, seq, d)
            x = x + o @ b_w_o[j]
        h = rms_norm(x, g_ffn[i])
        if i % 2 == 0:
            x = x + swiglu(h, ffn_w_gu[i // 2], ffn_w_down[i // 2])
        else:
            m = i // 2
            y = moe_swiglu(h.reshape(bsz * seq, d), moe_w_router[m], moe_w_gu[m], moe_w_down[m])
            x = x + y.reshape(bsz, seq, d)
    return rms_norm(x, g_final)


_drawn_inputs = setup_inputs


def setup_inputs(seed=0):
    import zlib

    import numpy as np

    out = dict(_drawn_inputs(seed))
    spreads = {}
    factors = {}
    for name, (base, spread) in spreads.items():
        noise = np.random.default_rng([zlib.crc32(name.encode()), seed]).standard_normal(out[name].shape)
        drawn = base * np.exp(spread * noise) if base else spread * noise
        out[name] = __import__('jax').numpy.asarray(drawn.astype(out[name].dtype))
    for name, factor in factors.items():
        out[name] = (out[name] * factor).astype(out[name].dtype)
    return out
```

```python
from contextlib import ExitStack

import concourse.bass as bass
from concourse import mybir

F32 = mybir.dt.float32
F32R = mybir.dt.float32r
I32 = mybir.dt.int32
ALU = mybir.AluOpType
ACT = mybir.ActivationFunctionType
AX = mybir.AxisListType

P = 128
SEQ = 256
D = 1024
KT = D // P
TT = SEQ // P
F = 2816
FC = 256
STEPS = F // FC
NH = 16
HD = D // NH
NE = 8
EPS = 1e-6
UNIT = 2048
HALF = UNIT // 2
RAW = 11
SPLIT = 6
MAX_ITEMS = NE + 3

U_WIN = 0
U_WOUT = U_WIN + 12
U_FFN = U_WOUT + 4
U_V = U_FFN + 3 * STEPS
U_K = U_V + 4
U_Q = U_K + 4
U_WO = U_Q + 4
U_MOE = U_WO + 4
ITEM_UNITS = 3 * STEPS
SLOTS_STATIC = {
    **{U_WIN + u: u % 3 for u in range(12)},
    **{U_WOUT + u: 3 + u for u in range(4)},
    **{U_FFN + u: u % 3 for u in range(3 * STEPS)},
    **{U_V + u: 3 + u for u in range(4)},
    **{U_K + u: u for u in range(4)},
    **{U_Q + u: (4, 5, 0, 1)[u] for u in range(4)},
    **{U_WO + u: 2 + u for u in range(4)},
}
SLOTS_MOE = (0, 1, 6, 7, 8, 9, 10, 2, 3, 4, 5)


def slot_of(u):
    return SLOTS_STATIC[u] if u < U_MOE else SLOTS_MOE[(u - U_MOE) % RAW]


def landed(u):
    return 32 * (sum(1 for v in range(u + 1) if slot_of(v) == slot_of(u)))


def prev_on_slot(u):
    found = [v for v in range(u) if slot_of(v) == slot_of(u)]
    return found[-1] if found else None


def lin(reg, by, const):
    return const + by * reg if isinstance(reg, int) else reg * by + const


ITEM_ORDER = [("gu", 0, 0), ("gu", 0, 1)]
for _j in range(1, STEPS):
    ITEM_ORDER += [("gu", _j, 0), ("gu", _j, 1), ("down", _j - 1, 0)]
ITEM_ORDER += [("down", STEPS - 1, 0)]

ACT_FFN = TT * STEPS
TR_NORMS = 4 * 4
HT_NORMS = 5 * 4
FIRST_QUARTERS = (0, 2, 1, 3)
Z_BANK = [4, 6, 2, 4, 6, 2, 4, 6]
SCATTER_STEP = (0, 2)
ONEHOT_T_STEP = 4
ONEHOT_STEP = 5
GATHER_STEP = 7
GATHER_T_STEP = 9


def tile_after(n):
    kind, j, part = ITEM_ORDER[n]
    if kind == "gu" and j == 1:
        return 0 if part == 0 else None
    if kind == "gu" and part == 1:
        return j if j == STEPS - 1 else None
    return j + 1 if kind == "down" and j < STEPS - 2 else None


def trunk(nc, x_in, g_mix, g_ffn, g_final, w_in, conv_w, w_out, g_kv, w_kv, w_q, w_o,
          ffn_gu, ffn_down, w_router, moe_gu, moe_down, out):
    with ExitStack() as ctx:
        def sb(name, shape, dt=F32):
            return ctx.enter_context(nc.sbuf_tensor(name, shape, dt))

        def sem(name):
            return ctx.enter_context(nc.semaphore(name))

        raw = sb("raw", [P, RAW * UNIT])
        whi = sb("whi", [P, SPLIT * HALF], F32R)
        wlo = sb("wlo", [P, SPLIT * HALF], F32R)
        x = sb("x", [P, TT, D])
        xq = sb("xq", [P, TT, D])
        hT_hi = sb("hT_hi", [P, TT, KT, P], F32R)
        hT_lo = sb("hT_lo", [P, TT, KT, P], F32R)
        mix_hi = sb("mix_hi", [P, UNIT], F32R)
        mix_lo = sb("mix_lo", [P, UNIT], F32R)
        hTf = sb("hTf", [P, 2, 512])
        act_sb = sb("act_sb", [P, 2, FC])
        actT_hi = sb("actT_hi", [P, 2, FC], F32R)
        actT_lo = sb("actT_lo", [P, 2, FC], F32R)
        ident = sb("ident", [P, P])
        neg_upto = sb("neg_upto", [P, P], F32R)
        neg_all = sb("neg_all", [P, P], F32R)
        before = sb("before", [P, P])
        ones = sb("ones", [P, P])
        iota = sb("iota", [P, P])
        rrow = sb("rrow", [P, SEQ])
        rrow2 = sb("rrow2", [P, SEQ])
        onehot = sb("onehot", [P, TT, P])
        onehot_r = sb("onehot_r", [P, TT, P], F32R)
        onehotT = sb("onehotT", [P, TT, P], F32R)
        vecT = sb("vecT", [P, 64])
        small = sb("small", [P, 640])

        taken = [0]

        def cut(n, *shape):
            at = taken[0]
            taken[0] += n
            v = small[:, at:at + n]
            if len(shape) == 2:
                v = v.rearrange("p (a b) -> p a b", a=shape[0])
            return v

        eps_col = cut(1)
        ssq, std, rstd = cut(10, 5, 2), cut(10, 5, 2), cut(10, 5, 2)
        rstd_slot = cut(1)
        logits, ismax, nmax = cut(16, 2, 8), cut(2), cut(2)
        rank, sel, den, rden = cut(16, 2, 8), cut(16, 2, 8), cut(2), cut(2)
        tap_now = cut(6, 3, 2)
        pair_gt, pair_eq = (cut(128).rearrange("p (t a b) -> p t a b", t=TT, a=NE) for _ in range(2))
        lower8 = cut(64, 8, 8)
        over, overpos = cut(8), cut(8)
        overhot = cut(24, 3, 8)
        item_pos, item_gate = cut(24, 2, 12), cut(24, 2, 12)
        pos_now, gate_now = cut(2), cut(2)
        table = cut(4)
        score, expo = cut(16, 2, 8), cut(16, 2, 8)
        scr8 = cut(24, 3, 8)
        iota_i = sb("iota_i", [P, P], I32)
        table_i = sb("table_i", [P, 4], I32)
        rw = sb("rw", [P, KT, NE])
        rw_hi = sb("rw_hi", [P, KT * NE + P], F32R)
        rw_lo = sb("rw_lo", [P, KT * NE + P], F32R)
        logitsT = act_sb[0:NE, 0, :]

        conv_c = raw[:, 9 * UNIT:9 * UNIT + 512].rearrange("p (c n) -> p c n", c=2)
        conv_u = raw[:, 9 * UNIT + 512:9 * UNIT + 512 + 2 * 258].rearrange("p (c n) -> p c n", c=2)
        conv_a = raw[:, 10 * UNIT:10 * UNIT + 512].rearrange("p (c n) -> p c n", c=2)
        conv_b = raw[:, 10 * UNIT + 512:10 * UNIT + 1024].rearrange("p (c n) -> p c n", c=2)
        vrows = raw[0:64, 8 * UNIT:8 * UNIT + P]
        ATT = 7 * UNIT
        lpart = [raw[:, ATT + 768 * b:ATT + 768 * (1 + b)].rearrange("p (h n) -> p h n", h=2) for b in range(2)]
        wpart = [raw[:, ATT + 768 * (2 + b):ATT + 768 * (3 + b)].rearrange("p (h n) -> p h n", h=2) for b in range(2)]
        g_row = raw[:, 5 * UNIT:5 * UNIT + D]
        oT = raw[:, 6 * UNIT:7 * UNIT].rearrange("p (c n) -> p c n", c=KT)
        kT = raw[:, 9 * UNIT:10 * UNIT].rearrange("p (c n) -> p c n", c=KT)
        vtok = raw[:, 10 * UNIT:11 * UNIT].rearrange("p (s n) -> p s n", s=TT)
        qT = xq[:, :, :].rearrange("p a b -> p (a b)").rearrange("p (c n) -> p c n", c=KT)
        hflat_hi = hT_hi[:, :, :, :].rearrange("p a b c -> p (a b c)")
        hflat_lo = hT_lo[:, :, :, :].rearrange("p a b c -> p (a b c)")
        l_hi = [hflat_hi[:, 768 * b:768 * (b + 1)].rearrange("p (h n) -> p h n", h=2) for b in range(2)]
        l_lo = [hflat_lo[:, 768 * b:768 * (b + 1)].rearrange("p (h n) -> p h n", h=2) for b in range(2)]
        drop = onehot_r
        ident_r = onehotT[:, 0, :]
        hq_hi = mix_hi[:, :].rearrange("p (t k n) -> p t k n", t=TT, k=KT)
        hq_lo = mix_lo[:, :].rearrange("p (t k n) -> p t k n", t=TT, k=KT)
        y_hi, y_lo = hflat_hi[:, D:2 * D], hflat_lo[:, D:2 * D]
        mixT_hi = mix_hi[:, :].rearrange("p (c n) -> p c n", c=KT)
        mixT_lo = mix_lo[:, :].rearrange("p (c n) -> p c n", c=KT)
        xs_hi = mix_hi[:, :].rearrange("p (a n) -> p a n", a=TT)
        xs_lo = mix_lo[:, :].rearrange("p (a n) -> p a n", a=TT)

        def two(row):
            return row.rearrange("p (a n) -> p a n", a=2)

        ps = ctx.enter_context(nc.psum_tensor("ps", [P, 8, 512], F32))

        GAIN = {"mix0": 0, "mix1": 8, "ffn0": 16, "ffn1": 24, "kv": 32}
        TAP = 40

        def gain_of(which, quarter_bank):
            at = GAIN[which] + 4 * quarter_bank
            return vecT[:, at:at + 4].unsqueeze(2).to_broadcast([P, 4, P])

        raw_in = [sem(f"raw_in{s}") for s in range(RAW)]
        hi_done, lo_done = sem("hi_done"), sem("lo_done")
        half_used = sem("half_used")
        x_in_s, vec_in, rw_in, gr_in, gf_in, out_s = (
            sem("x_in"), sem("vec_in"), sem("rw_in"), sem("gr_in"), sem("gf_in"), sem("out_s"))
        ident_done, const_done = sem("ident_done"), sem("const_done")
        vecT_ps, vecT_done = sem("vecT_ps"), sem("vecT_done")
        y0_done, x_ready = sem("y0_done"), sem("x_ready")
        std_done, rstd_done, rrow_ps, rrow_done = sem("std_done"), sem("rstd_done"), sem("rrow_ps"), sem("rrow_done")
        diag_done = sem("diag_done")
        tr_done = sem("tr_done")
        hm_done, hh_done, ht_done = sem("hm_done"), sem("hh_done"), sem("ht_done")
        c_copied, conv_done, ch_done, cl_done = sem("c_copied"), sem("conv_done"), sem("ch_done"), sem("cl_done")
        silu_done, act_done = sem("silu_done"), sem("act_done")
        at_done, ah_done, al_done = sem("at_done"), sem("ah_done"), sem("al_done")
        kq_copied, v_copied = sem("kq_copied"), sem("v_copied")
        z_done, l_done, m_done = sem("z_done"), sem("l_done"), sem("m_done")
        lh_done, ll_done, s_done = sem("lh_done"), sem("ll_done"), sem("s_done")
        p_done, o_done, o_copied = sem("p_done"), sem("o_done"), sem("o_copied")
        oh_done, ol_done = sem("oh_done"), sem("ol_done")
        gx_done, xs_hi_done, xs_done = sem("gx_done"), sem("xs_hi_done"), sem("xs_done")
        rh_done, rl_done = sem("rh_done"), sem("rl_done")
        lT_ps, lT_done, rslot_ps, rslot_done = sem("lT_ps"), sem("lT_done"), sem("rslot_ps"), sem("rslot_done")
        logits_ps, nmax_done, expo_done, sel_done, pos_ps, tbl_done = (
            sem("logits_ps"), sem("nmax_done"), sem("expo_done"), sem("sel_done"), sem("pos_ps"), sem("tbl_done"))
        xg_ps, xg_done = sem("xg_ps"), sem("xg_done")
        oneh_done, onehT_ps, onehT_done = sem("oneh_done"), sem("onehT_ps"), sem("onehT_done")
        yh_done, yl_done, sc_done, comb_done = sem("yh_done"), sem("yl_done"), sem("sc_done"), sem("comb_done")
        out_done = sem("out_done")

        def slot(s):
            return raw[:, s * UNIT:(s + 1) * UNIT]

        def cols_src(w, c0):
            return w.rearrange("(k p) n -> p k n", p=P)[:, :, bass.ds(c0, 256)]

        def rows_src(w, k):
            return w.rearrange("(c t p) n -> c p t n", t=2, p=P)[k]

        def gu_src(w, j, part):
            return w.rearrange("(k p) (g n) -> p k g n", p=P, g=2)[:, 4 * part:4 * part + 4, :, bass.ds(j * FC, FC)]

        def ring(at):
            return slice((at % SPLIT) * HALF, (at % SPLIT + 1) * HALF)

        block = ctx.enter_context(nc.Block())

        @block.sync
        def _(sp):
            def load(u, src, reg=0, units=0):
                s = slot_of(u)
                prev = u - RAW if u >= U_MOE + RAW or units == ITEM_UNITS else prev_on_slot(u)
                if prev is not None:
                    sp.wait_ge(lo_done, lin(reg, 2 * units, 2 * prev + 2))
                if len(src.shape) == 4:
                    dst = slot(s).rearrange("p (k g n) -> p k g n", g=2, n=FC)
                    for g in range(2):
                        sp.dma_start(dst[:, :, g, :], src[:, :, g, :]).then_inc(raw_in[s], 16)
                else:
                    n = src.shape[1]
                    dst = slot(s).rearrange("p (k n) -> p k n", k=n)
                    for g in range(2):
                        part = slice(g * n // 2, (g + 1) * n // 2)
                        sp.dma_start(dst[:, part, :], src[:, part, :]).then_inc(raw_in[s], 16)

            row = 0
            for src in (g_mix.rearrange("a (k p) -> (a k) p", p=P), g_ffn.rearrange("a (k p) -> (a k) p", p=P),
                        g_kv.rearrange("(k p) -> k p", p=P), conv_w[0].rearrange("a (k p) -> (a k) p", p=P)):
                n = src.shape[0]
                sp.dma_start(raw[row:row + n, 8 * UNIT:8 * UNIT + P], src).then_inc(vec_in, 16)
                row += n
            for t in range(TT):
                sp.dma_start(x[:, t], x_in[0, t * P:(t + 1) * P, :]).then_inc(x_in_s, 16)
            for c in range(3):
                load(U_WIN + c, cols_src(w_in[0], c * D))
            with sp.Fori(0, 3) as r:
                for c in range(3):
                    load(U_WIN + 3 + c, cols_src(w_in[0], r * 256 + (c * D + 256)), r, 3)
            for k in range(4):
                load(U_WOUT + k, rows_src(w_out[0], k))
            sp.dma_start(rw[:, :, :], w_router[0].rearrange("(k p) e -> p k e", p=P)).then_inc(rw_in, 16)
            load(U_FFN, gu_src(ffn_gu[0], 0, 0))
            load(U_FFN + 1, gu_src(ffn_gu[0], 0, 1))
            load(U_FFN + 2, gu_src(ffn_gu[0], 1, 0))
            load(U_FFN + 3, gu_src(ffn_gu[0], 1, 1))
            load(U_FFN + 4, rows_src(ffn_down[0], 0))
            with sp.Fori(0, STEPS - 2) as r:
                load(U_FFN + 5, gu_src(ffn_gu[0], r + 2, 0), r, 3)
                load(U_FFN + 6, gu_src(ffn_gu[0], r + 2, 1), r, 3)
                load(U_FFN + 7, rows_src(ffn_down[0], r + 1), r, 3)
            load(U_V - 1, rows_src(ffn_down[0], STEPS - 1))
            for k in range(4):
                load(U_V + k, rows_src(w_kv[:, D:2 * D], k))
            for k in range(4):
                load(U_K + k, cols_src(w_kv, 256 * k))
            for k in range(4):
                load(U_Q + k, cols_src(w_q[0], 256 * k))
            for k in range(4):
                load(U_WO + k, rows_src(w_o[0], k))

            def item(gu_w, down_w, i, order=ITEM_ORDER, first=False):
                for n, (kind, j, part) in enumerate(order):
                    if first and n < RAW and slot_of(U_MOE + n) == 6:
                        sp.wait_ge(lo_done, 2 * (U_WO + 3) + 2)
                        sp.dma_start(g_row, g_ffn[1:2, :].to_broadcast([P, D])).then_inc(gr_in, 16)
                        sp.wait_ge(ol_done, 4)
                    if first and slot_of(U_MOE + n) == 5 and n < RAW:
                        sp.wait_ge(gx_done, TT)
                    load(U_MOE + n, gu_src(gu_w, j, part) if kind == "gu" else rows_src(down_w, j),
                         0 if first else i, 0 if first else ITEM_UNITS)

            item(moe_gu[0, 0], moe_down[0, 0], 0, first=True)
            with sp.Fori(1, NE) as i:
                item(moe_gu[0][i], moe_down[0][i], i)
            sp.wait_ge(tbl_done, 1)
            items = sp.value_load(table_i[0:1, 0:1], min_val=NE, max_val=MAX_ITEMS)
            with sp.If(items > NE):
                with sp.Fori(NE, items) as i:
                    e = sp.value_load(table_i[0:1, bass.ds(i - (NE - 1), 1)], min_val=0, max_val=NE - 1)
                    item(moe_gu[0][e], moe_down[0][e], i)
            item(moe_gu[0, 0], moe_down[0, 0], items, order=ITEM_ORDER[:3])
            sp.dma_start(xq[:, 0, :], g_final.rearrange("(a n) -> a n", a=1).to_broadcast([P, D])).then_inc(gf_in, 16)
            for t in range(TT):
                sp.wait_ge(out_done, t + 1)
                sp.dma_start(out[0, t * P:(t + 1) * P, :], x[:, t]).then_inc(out_s, 16)
            sp.wait_ge(out_s, 16 * TT)

        @block.gpsimd
        def _(pool):
            pool.memset(ident[:, :], 0.0)
            pool.drain()
            pool.affine_select(out=ident[:, :], in_=ident[:, :], compare_op=ALU.not_equal, fill=1.0,
                               base=0, pattern=[[-1, P]], channel_multiplier=1).then_inc(ident_done, 1)
            pool.memset(ones[:, :], 1.0)
            pool.memset(eps_col, EPS)
            pool.memset(conv_u[:, :, 0:2], 0.0)
            pool.memset(rw_hi[:, :].bitcast(F32), 0.0)
            pool.memset(rw_lo[:, :].bitcast(F32), 0.0)
            pool.memset(lower8, 1.0)
            pool.memset(act_sb[:, 0, 0:P], -1.0)
            pool.memset(item_pos, 0.0)
            pool.memset(item_gate, 0.0)
            pool.iota(iota_i[:, :], pattern=[[1, P]], base=1, channel_multiplier=0)
            pool.drain()
            pool.affine_select(out=before[:, :], in_=ones[:, :], compare_op=ALU.is_gt, fill=0.0,
                               base=0, pattern=[[1, P]], channel_multiplier=-1)
            pool.affine_select(out=lower8, in_=lower8, compare_op=ALU.is_gt, fill=0.0,
                               base=0, pattern=[[1, 8], [-1, 8]], channel_multiplier=0)
            pool.affine_select(out=act_sb[:, 0, P:2 * P], in_=act_sb[:, 0, 0:P], compare_op=ALU.is_ge, fill=0.0,
                               base=0, pattern=[[-1, P]], channel_multiplier=1)
            pool.tensor_copy(iota[:, :], iota_i[:, :])
            pool.drain()
            pool.tensor_copy(neg_all[:, :], act_sb[:, 0, 0:P])
            pool.tensor_copy(neg_upto[:, :], act_sb[:, 0, P:2 * P])
            pool.tensor_copy(ident_r, ident[:, :])
            for t in range(2):
                pool.tensor_scalar(drop[:, t], before[:, :], -1.0, 1e30, ALU.add, ALU.mult)
            pool.drain()
            pool.memset(scr8[:, 0, 0:1], 0.0).then_inc(const_done, 1)

        @block.scalar
        def _(act):
            def split(u, reg=0, units=0, loads=0, halves=(0, 1)):
                s = slot_of(u)
                act.wait_ge(raw_in[s], lin(reg, 32 * loads, landed(u)))
                for h in halves:
                    at = 2 * u + h
                    if at >= SPLIT:
                        act.wait_ge(half_used, lin(reg, 2 * units, at - SPLIT + 1))
                    act.activation(whi[:, ring(at)], slot(s)[:, h * HALF:(h + 1) * HALF],
                                   ACT.Copy).then_inc(hi_done, 1)

            def square(n, t, scratch):
                act.activation(scratch, two(x[:, t]), ACT.Square, accum_out=ssq[:, n, t:t + 1])
                act.drain()

            def deviation(n):
                act.activation(std[:, n], ssq[:, n], ACT.Sqrt, bias=eps_col, scale=1.0 / D).then_inc(std_done, 1)

            def h_quarter(n, q, reg=0, to=hT_hi):
                act.wait_ge(hm_done, lin(reg, 2, n + 1))
                act.activation(to[:, q // 2, 4 * (q % 2):4 * (q % 2) + 4, :],
                               hTf[:, n % 2, :].rearrange("p (k n) -> p k n", k=4), ACT.Copy).then_inc(hh_done, 1)

            def silu(gate_up_unit, bank, buf, scale, reg=0, units=0):
                act.wait_ge(half_used, lin(reg, 2 * units, 2 * gate_up_unit + 2))
                act.activation(act_sb[:, buf, :], ps[:, bank, 0:FC], ACT.Silu, scale=scale).then_inc(silu_done, 1)

            def act_high(n, bank, buf, reg=0, tiles=0):
                act.wait_ge(at_done, lin(reg, tiles, n + 1))
                act.activation(actT_hi[:, buf, :], ps[:, bank, 0:FC], ACT.Copy).then_inc(ah_done, 1)

            def conv_high(m, reg=0):
                act.wait_ge(conv_done, lin(reg, 1, m + 1))
                act.activation(mix_hi[:, bass.ds(lin(reg, 512, 512 * m), 512)], conv_a.rearrange("p c n -> p (c n)"),
                               ACT.Copy).then_inc(ch_done, 1)

            for h in range(2):
                for n in (2 * h, 2 * h + 1):
                    h_quarter(n, FIRST_QUARTERS[n])
                split(U_WIN, halves=(h,))
            act.wait_ge(const_done, 1)
            act.wait_ge(x_in_s, 16 * TT)
            for t in range(TT):
                square(0, t, two(xq[:, t]))
            deviation(0)
            split(U_WIN + 1)
            split(U_WIN + 2)
            with act.Fori(0, 3) as r:
                split(U_WIN + 3, r, 3, 1)
                split(U_WIN + 4, r, 3, 1)
                conv_high(0, r)
                split(U_WIN + 5, r, 3, 1)
            split(U_WOUT)
            split(U_WOUT + 1)
            conv_high(3)
            split(U_WOUT + 2)
            split(U_WOUT + 3)
            split(U_FFN)
            act.wait_ge(x_ready, 2)
            square(1, 0, two(xq[:, 0]))
            for q in range(2):
                h_quarter(4 + q, q)
            split(U_FFN + 1)
            act.wait_ge(x_ready, 4)
            square(1, 1, two(xq[:, 1]))
            for q in range(2, 4):
                h_quarter(4 + q, q)
            deviation(1)
            act.wait_ge(rw_in, 16)
            act.activation(rw_hi[:, 0:KT * NE], rw[:, :, :].rearrange("p k e -> p (k e)"), ACT.Copy).then_inc(rh_done, 1)
            act.wait_ge(rstd_done, 2)

            def ffn_step(r, tile_unit):
                split(U_FFN + 2, r, 3, 1)
                split(U_FFN + 3, r, 3, 1)
                for b in range(TT):
                    silu(tile_unit, 4 + b, b, rstd[:, 1, b:b + 1], r, 3)
                split(U_FFN + 4, r, 3, 1)
                for b in range(TT):
                    act_high(b, 6 + b, b, r, TT)

            ffn_step(0, U_FFN + 1)
            with act.Fori(1, STEPS - 1) as r:
                ffn_step(r, U_FFN)
            split(U_V - 1)
            split(U_V)
            for b in range(TT):
                silu(U_V - 3, 4 + b, b, rstd[:, 1, b:b + 1])
            act_high(TT * (STEPS - 1), 6, 0)
            split(U_V + 1)
            act_high(TT * (STEPS - 1) + 1, 7, 1)
            act.wait_ge(x_ready, 6)
            square(2, 0, two(xq[:, 0]))
            for q in range(2):
                h_quarter(8 + q, q)
            split(U_V + 2)
            act.wait_ge(x_ready, 8)
            square(2, 1, two(xq[:, 1]))
            for q in range(2, 4):
                h_quarter(8 + q, q)
            deviation(2)
            split(U_V + 3)
            for q in range(2):
                h_quarter(12 + q, q, to=hq_hi)
            split(U_K)
            for q in range(2, 4):
                h_quarter(12 + q, q, to=hq_hi)
            split(U_K + 1)
            act.wait_ge(rstd_done, 3)
            act.wait_ge(half_used, 2 * U_V + 8)
            for q in range(4):
                act.activation(vtok[:, q // 2, 512 * (q % 2):512 * (q % 2) + 512], ps[:, 4 + q, :], ACT.Copy,
                               scale=rstd[:, 2, q // 2:q // 2 + 1]).then_inc(v_copied, 1)
            for u in range(U_K + 2, U_WO):
                split(u)

            act.preload_act_table_set("natural_log_exp_and_others")

            def softplus_tail(c):
                act.wait_ge(z_done, c + 1)
                if c >= 2:
                    act.wait_ge(ll_done, c - 1)
                act.activation(lpart[c % 2], ps[:, Z_BANK[c]:Z_BANK[c] + 2, 0:384], ACT.Abs)
                act.drain()
                act.activation(lpart[c % 2], lpart[c % 2], ACT.Exp, scale=-1.0)
                act.drain()
                act.activation(lpart[c % 2], lpart[c % 2], ACT.Ln, bias=1.0).then_inc(l_done, 1)

            def attention_weights(c):
                act.wait_ge(s_done, c + 1)
                if c >= 2:
                    act.wait_ge(o_done, c - 1)
                act.activation(wpart[c % 2], ps[:, Z_BANK[c]:Z_BANK[c] + 2, 0:384], ACT.Exp).then_inc(p_done, 1)

            def out_high(k):
                act.wait_ge(o_copied, 2 * k + 2)
                act.activation(mixT_hi[:, 2 * k:2 * k + 2, :], oT[:, 2 * k:2 * k + 2, :], ACT.Copy).then_inc(oh_done, 1)

            for r in range(KT + 1):
                if r < KT:
                    softplus_tail(r)
                if r >= 1:
                    attention_weights(r - 1)
                if 1 <= r <= 3:
                    split(U_WO + r - 1)
                if r in (4, 6, 8):
                    out_high(r // 2 - 2)
            out_high(3)
            split(U_WO + 3)
            split(U_MOE)
            split(U_MOE + 1)
            act.wait_ge(x_ready, 10)
            square(3, 0, ps[:, 4:6, :])
            for q in range(2):
                h_quarter(16 + q, q)
            act.wait_ge(x_ready, 12)
            square(3, 1, ps[:, 4:6, :])
            for q in range(2, 4):
                h_quarter(16 + q, q)
            deviation(3)
            for t in range(TT):
                act.wait_ge(gx_done, t + 1)
                act.activation(xs_hi[:, t], xq[:, t], ACT.Copy).then_inc(xs_hi_done, 1)
            act.preload_act_table(ACT.Exp)
            split(U_MOE + 2)
            act.wait_ge(nmax_done, 1)
            for t in range(TT):
                act.activation(expo[:, t], logits[:, t], ACT.Exp, bias=nmax[:, t:t + 1]).then_inc(expo_done, 1)

            def slot_rstd():
                act.activation(rstd_slot, ps[:, 5, 0:1], ACT.Copy).then_inc(rslot_done, 1)

            def gathered(item):
                for q in range(2):
                    act.wait_ge(xg_ps, lin(item, 2, q + 1))
                    act.activation(hTf[:, q, :], ps[:, 2 + q, :], ACT.Copy).then_inc(xg_done, 1)

            def item_high(item):
                act.wait_ge(tr_done, lin(item, 2, TR_NORMS + 2))
                act.activation(hflat_hi[:, 0:D].rearrange("p (a n) -> p a n", a=2), ps[:, 2:4, :],
                               ACT.Copy).then_inc(hh_done, 1)

            act.wait_ge(ht_done, HT_NORMS)
            gathered(0)
            act.preload_act_table(ACT.Silu)
            item_high(0)
            act.wait_ge(rslot_ps, 1)
            slot_rstd()
            act.activation(onehotT[:, 0, :], ident[:, :], ACT.Copy, scale=0.0)
            act.activation(onehotT[:, 1, :], ident[:, :], ACT.Copy, scale=0.0).then_inc(onehT_done, 1)
            act.wait_ge(tbl_done, 1)
            items = act.value_load(table_i[0:1, 0:1], min_val=NE, max_val=MAX_ITEMS)
            with act.Fori(0, items) as i:
                for n in range(3, ITEM_UNITS + 3):
                    kind, j, part = ITEM_ORDER[n - 3]
                    split(U_MOE + n, i, ITEM_UNITS, 3, (0,))
                    if n == ITEM_UNITS + 2:
                        act.wait_ge(half_used, i * (2 * ITEM_UNITS) + 2 * (U_MOE + ITEM_UNITS))
                        act.activation(two(y_hi), ps[:, 0:2, :], ACT.Copy).then_inc(yh_done, 1)
                    if kind == "gu" and part == 1 and j == 0:
                        act.wait_ge(rslot_done, i + 1)
                    if kind == "gu" and part == 1:
                        silu(U_MOE + n - 3, 4 + j % 2, j % 2, rstd_slot, i, ITEM_UNITS)
                    split(U_MOE + n, i, ITEM_UNITS, 3, (1,))
                    done = tile_after(n - 3)
                    if done is not None:
                        act_high(ACT_FFN + done, 6 + done % 2, done % 2, i, STEPS)
                    if kind == "gu" and part == 1 and j == ONEHOT_T_STEP:
                        act.wait_ge(onehT_ps, i + 1)
                        act.activation(onehotT[:, :, :].rearrange("p a b -> p (a b)"), ps[:, 3, 0:2 * P],
                                       ACT.Copy).then_inc(onehT_done, 1)
                    if kind == "down" and j == GATHER_STEP - 1:
                        gathered(i + 1)
                    if kind == "gu" and part == 1 and j == STEPS - 1:
                        item_high(i + 1)
                        act.wait_ge(rslot_ps, i + 2)
                        act.wait_ge(act_done, i * STEPS + (ACT_FFN + STEPS))
                        slot_rstd()
            act.preload_act_table(ACT.Sqrt)
            for t in range(TT):
                act.wait_ge(comb_done, items * TT + (t + 1))
                square(4, t, hTf[:, :, :])
                act.activation(std[:, 4, t:t + 1], ssq[:, 4, t:t + 1], ACT.Sqrt, bias=eps_col,
                               scale=1.0 / D).then_inc(std_done, 1)

        @block.vector
        def _(dve):
            def split(u, reg=0, units=0, halves=(0, 1)):
                s = slot_of(u)
                for h in halves:
                    at = 2 * u + h
                    dve.wait_ge(hi_done, lin(reg, 2 * units, at + 1))
                    dve.tensor_tensor(wlo[:, ring(at)], slot(s)[:, h * HALF:(h + 1) * HALF], whi[:, ring(at)],
                                      ALU.subtract).then_inc(lo_done, 1)

            def inverse(n):
                dve.wait_ge(std_done, n + 1)
                dve.reciprocal(rstd[:, n], std[:, n]).then_inc(rstd_done, 1)

            def diagonals(n):
                dve.wait_ge(rstd_done, n + 1)
                for t in range(TT):
                    last = dve.tensor_scalar(onehot[:, t], ident[:, :], rstd[:, n, t:t + 1], None, ALU.mult)
                    last.then_inc(diag_done, 1)

            def rows(n):
                dve.wait_ge(rrow_ps, n)
                dve.tensor_copy(rrow[:, :], ps[:, 3, 0:SEQ]).then_inc(rrow_done, 1)
                dve.wait_ge(rrow_done, n)

            def scale_quarter(n, bank, gain, q, reg=0, tr=0):
                dve.wait_ge(tr_done, lin(reg, 2, tr + 1))
                if n >= 2:
                    dve.wait_ge(ht_done, lin(reg, 2, n - 1))
                dve.tensor_tensor(hTf[:, n % 2, :].rearrange("p (k n) -> p k n", k=4),
                                  ps[:, bank, :].rearrange("p (k n) -> p k n", k=4), gain_of(gain, q % 2),
                                  ALU.mult).then_inc(hm_done, 1)

            def low_quarter(n, q, reg=0, to=(hT_hi, hT_lo)):
                dve.wait_ge(hh_done, lin(reg, 2, n + 1))
                k = 4 * (q % 2)
                dve.tensor_tensor(to[1][:, q // 2, k:k + 4, :], hTf[:, n % 2, :].rearrange("p (k n) -> p k n", k=4),
                                  to[0][:, q // 2, k:k + 4, :], ALU.subtract).then_inc(ht_done, 1)

            def quarter_pair(n, tr, q0, gain, to=(hT_hi, hT_lo)):
                for q in (q0, q0 + 1):
                    scale_quarter(n + q, q, gain, q, tr=tr + q)
                for q in (q0, q0 + 1):
                    low_quarter(n + q, q, to=to)

            def mult(n, bank, buf, scale, reg=0, tiles=0):
                dve.wait_ge(silu_done, lin(reg, tiles, n + 1))
                dve.scalar_tensor_tensor(act_sb[:, buf, :], ps[:, bank, FC:2 * FC], scale, act_sb[:, buf, :],
                                         ALU.mult, ALU.mult).then_inc(act_done, 1)

            def act_low(n, bank, buf, reg=0, tiles=0):
                dve.wait_ge(ah_done, lin(reg, tiles, n + 1))
                dve.tensor_tensor(actT_lo[:, buf, :], ps[:, bank, 0:FC], actT_hi[:, buf, :],
                                  ALU.subtract).then_inc(al_done, 1)

            def add_result(u, n, t):
                if t == 0:
                    dve.wait_ge(y0_done, n + 1)
                else:
                    dve.wait_ge(half_used, 2 * u + 2)
                for c in range(2):
                    xs = x[:, t, 512 * c:512 * c + 512]
                    dve.tensor_tensor(xs, xs, ps[:, 2 * t + c, :], ALU.add).then_inc(x_ready, 1)

            def conv(m, reg=0):
                dve.tensor_copy(tap_now, vecT[:, TAP:TAP + 24].rearrange("p (t c) -> p t c", t=3)[
                    :, :, bass.ds(lin(reg, 2, 2 * m), 2)])
                dve.wait_ge(half_used, lin(reg, 6, 6 * m + 2))
                dve.tensor_tensor(conv_c, ps[:, 4, :].rearrange("p (c n) -> p c n", c=2),
                                  rrow2[:, :].unsqueeze(1).to_broadcast([P, 2, SEQ]), ALU.mult).then_inc(c_copied, 1)
                dve.wait_ge(c_copied, lin(reg, 1, m + 1))
                dve.wait_ge(half_used, lin(reg, 6, 6 * m + 4))
                dve.tensor_tensor(conv_u[:, :, 2:258], conv_c, ps[:, 5, :].rearrange("p (c n) -> p c n", c=2), ALU.mult)
                dve.drain()
                if not (isinstance(reg, int) and m == 0):
                    dve.wait_ge(ch_done, lin(reg, 1, m))
                for c in range(2):
                    dve.tensor_scalar(conv_a[:, c], conv_u[:, c, 0:SEQ], tap_now[:, 0, c:c + 1], None, ALU.mult)
                dve.drain()
                for c in range(2):
                    dve.scalar_tensor_tensor(conv_b[:, c], conv_u[:, c, 1:SEQ + 1], tap_now[:, 1, c:c + 1], conv_a[:, c],
                                             ALU.mult, ALU.add)
                dve.drain()
                for c in range(2):
                    dve.scalar_tensor_tensor(conv_a[:, c], conv_u[:, c, 2:SEQ + 2], tap_now[:, 2, c:c + 1], conv_b[:, c],
                                             ALU.mult, ALU.add)
                dve.drain()
                dve.tensor_tensor(conv_a, conv_a, rrow[:, :].unsqueeze(1).to_broadcast([P, 2, SEQ]), ALU.mult)
                dve.drain()

            def gate_b(m, reg=0):
                dve.wait_ge(half_used, lin(reg, 6, 6 * m + 6))
                dve.tensor_tensor(conv_a, conv_a, ps[:, 6, :].rearrange("p (c n) -> p c n", c=2),
                                  ALU.mult).then_inc(conv_done, 1)

            def conv_low(m, reg=0):
                dve.wait_ge(ch_done, lin(reg, 1, m + 1))
                at = bass.ds(lin(reg, 512, 512 * m), 512)
                dve.tensor_tensor(mix_lo[:, at], conv_a.rearrange("p c n -> p (c n)"), mix_hi[:, at],
                                  ALU.subtract).then_inc(cl_done, 1)

            dve.wait_ge(vecT_ps, 1)
            dve.tensor_copy(vecT[:, :], ps[:, 7, 0:64]).then_inc(vecT_done, 1)
            dve.wait_ge(vecT_done, 1)
            for h in range(2):
                for n in (2 * h, 2 * h + 1):
                    q = FIRST_QUARTERS[n]
                    scale_quarter(n, q, "mix0", q, tr=n)
                for n in (2 * h, 2 * h + 1):
                    low_quarter(n, FIRST_QUARTERS[n])
                split(U_WIN, halves=(h,))
            dve.wait_ge(const_done, 1)
            inverse(0)
            diagonals(0)
            split(U_WIN + 1)
            rows(1)
            dve.tensor_tensor(rrow2[:, :], rrow[:, :], rrow[:, :], ALU.mult)
            dve.drain()
            split(U_WIN + 2)
            with dve.Fori(0, 3) as r:
                split(U_WIN + 3, r, 3)
                conv(0, r)
                split(U_WIN + 4, r, 3)
                gate_b(0, r)
                split(U_WIN + 5, r, 3)
                conv_low(0, r)
                dve.drain()
            split(U_WOUT)
            conv(3)
            split(U_WOUT + 1)
            gate_b(3)
            split(U_WOUT + 2)
            conv_low(3)
            split(U_WOUT + 3)
            add_result(U_FFN - 1, 0, 0)
            split(U_FFN)
            quarter_pair(4, 4, 0, "ffn0")
            split(U_FFN + 1)
            add_result(U_FFN - 1, 0, 1)
            quarter_pair(4, 4, 2, "ffn0")
            inverse(1)
            dve.wait_ge(rh_done, 1)
            dve.tensor_tensor(rw_lo[:, 0:KT * NE], rw[:, :, :].rearrange("p k e -> p (k e)"), rw_hi[:, 0:KT * NE],
                              ALU.subtract).then_inc(rl_done, 1)

            def ffn_step(r):
                split(U_FFN + 2, r, 3)
                split(U_FFN + 3, r, 3)
                for b in range(TT):
                    mult(b, 4 + b, b, rstd[:, 1, b:b + 1], r, TT)
                split(U_FFN + 4, r, 3)
                for b in range(TT):
                    act_low(b, 6 + b, b, r, TT)

            with dve.Fori(0, STEPS - 1) as r:
                ffn_step(r)
            split(U_V - 1)
            split(U_V)
            for b in range(TT):
                mult(TT * (STEPS - 1) + b, 4 + b, b, rstd[:, 1, b:b + 1])
            act_low(TT * (STEPS - 1), 6, 0)
            split(U_V + 1)
            act_low(TT * (STEPS - 1) + 1, 7, 1)
            add_result(U_V - 1, 1, 0)
            quarter_pair(8, 8, 0, "kv")
            add_result(U_V - 1, 1, 1)
            split(U_V + 2)
            quarter_pair(8, 8, 2, "kv")
            inverse(2)
            diagonals(2)
            split(U_V + 3)
            quarter_pair(12, 8, 0, "mix1", (hq_hi, hq_lo))
            split(U_K)
            quarter_pair(12, 8, 2, "mix1", (hq_hi, hq_lo))

            def columns(u, n, bank, to, scale):
                dve.wait_ge(half_used, 2 * u + 2)
                dve.scalar_tensor_tensor(to[:, 2 * n:2 * n + 2, :], ps[:, bank, :].rearrange("p (c n) -> p c n", c=2),
                                         scale, rrow[:, :].unsqueeze(1).to_broadcast([P, 2, SEQ]), ALU.mult,
                                         ALU.mult).then_inc(kq_copied, 1)

            split(U_K + 1)
            split(U_K + 2)
            rows(2)
            for k in range(4):
                columns(U_K + k, k, k % 2, kT, 1.0)
                split(U_K + 3 + k)
            columns(U_Q, 0, 0, qT, HD ** -0.5)
            split(U_Q + 3)
            columns(U_Q + 1, 1, 1, qT, HD ** -0.5)

            def scores_of(c):
                return ps[:, Z_BANK[c]:Z_BANK[c] + 2, 0:384]

            def softplus(c):
                dve.wait_ge(l_done, c + 1)
                dve.scalar_tensor_tensor(lpart[c % 2], scores_of(c), 0.0, lpart[c % 2], ALU.max,
                                         ALU.add).then_inc(m_done, 1)

            def split_softplus(c):
                dve.wait_ge(m_done, c + 1)
                if c >= 2:
                    dve.wait_ge(s_done, c - 1)
                dve.tensor_copy(l_hi[c % 2], lpart[c % 2]).then_inc(lh_done, 1)
                dve.wait_ge(lh_done, c + 1)
                dve.tensor_tensor(l_lo[c % 2], lpart[c % 2], l_hi[c % 2], ALU.subtract).then_inc(ll_done, 1)

            def out_copy(c):
                dve.wait_ge(o_done, c + 1)
                dve.tensor_copy(oT[:, c, :], ps[:, Z_BANK[c], 0:SEQ]).then_inc(o_copied, 1)

            def out_low(k):
                dve.wait_ge(oh_done, k + 1)
                dve.tensor_tensor(mixT_lo[:, 2 * k:2 * k + 2, :], oT[:, 2 * k:2 * k + 2, :],
                                  mixT_hi[:, 2 * k:2 * k + 2, :], ALU.subtract).then_inc(ol_done, 1)

            for r in range(KT + 2):
                if r >= 2:
                    out_copy(r - 2)
                if r < KT:
                    softplus(r)
                    split_softplus(r)
                if r in (2, 4):
                    columns(U_Q + r // 2 + 1, r // 2 + 1, (r // 2 + 1) % 2, qT, HD ** -0.5)
                if 1 <= r <= 3:
                    split(U_WO + r - 1)
                if r in (5, 7):
                    out_low((r - 5) // 2)
            out_low(2)
            out_low(3)
            split(U_WO + 3)
            split(U_MOE)
            add_result(U_MOE - 1, 2, 0)

            def times_gain(t):
                dve.tensor_tensor(xq[:, t], x[:, t], g_row, ALU.mult).then_inc(gx_done, 1)

            dve.wait_ge(gr_in, 16)
            dve.wait_ge(x_ready, 10)
            times_gain(0)
            for q in range(2):
                scale_quarter(16 + q, q, "ffn1", q, tr=12 + q)
            add_result(U_MOE - 1, 2, 1)
            for q in range(2):
                low_quarter(16 + q, q)
            quarter_pair(16, 12, 2, "ffn1")
            times_gain(1)
            for t in range(TT):
                dve.wait_ge(xs_hi_done, t + 1)
                dve.tensor_tensor(xs_lo[:, t], xq[:, t], xs_hi[:, t], ALU.subtract).then_inc(xs_done, 1)
            dve.wait_ge(lT_ps, 1)
            dve.tensor_copy(logitsT, ps[0:NE, 6, 0:SEQ]).then_inc(lT_done, 1)
            inverse(3)
            dve.wait_ge(rstd_done, 4)
            dve.wait_ge(logits_ps, 1)
            for t in range(TT):
                dve.tensor_scalar(logits[:, t], ps[:, 7, NE * t:NE * (t + 1)], rstd[:, 3, t:t + 1], None, ALU.mult)
            dve.drain()
            mine = logits.unsqueeze(3).to_broadcast([P, TT, NE, NE])
            other = logits.unsqueeze(2).to_broadcast([P, TT, NE, NE])
            dve.tensor_tensor(pair_gt, other, mine, ALU.is_gt)
            dve.tensor_tensor(pair_eq, other, mine, ALU.is_equal)
            dve.drain()
            dve.tensor_tensor(pair_eq, pair_eq, lower8.unsqueeze(1).to_broadcast([P, TT, NE, NE]), ALU.mult)
            dve.drain()
            dve.tensor_tensor(pair_gt, pair_gt, pair_eq, ALU.add)
            dve.drain()
            dve.tensor_reduce(rank, pair_gt, AX.X, ALU.add)
            dve.drain()
            dve.tensor_scalar(sel, rank, 1.5, None, ALU.is_lt).then_inc(sel_done, 1)
            dve.tensor_reduce(ismax, logits, AX.X, ALU.max)
            dve.drain()
            dve.tensor_scalar(nmax, ismax, -1.0, None, ALU.mult).then_inc(nmax_done, 1)
            dve.wait_ge(sel_done, 1)
            dve.wait_ge(pos_ps, 1)
            place = ps[:, 7, 0:2 * NE].rearrange("p (t e) -> p t e", t=TT)
            dve.scalar_tensor_tensor(item_pos[:, :, 0:NE], place, 1.0, sel, ALU.add, ALU.mult)
            dve.drain()

            def one_hots(item):
                dve.tensor_copy(pos_now, item_pos[:, :, bass.ds(item, 1)].rearrange("p t o -> p (t o)"))
                dve.drain()
                for t in range(TT):
                    dve.tensor_scalar(onehot[:, t], iota[:, :], pos_now[:, t:t + 1], None, ALU.is_equal)
                dve.drain()
                dve.tensor_copy(onehot_r[:, :, :], onehot[:, :, :]).then_inc(oneh_done, 1)

            def item_low(item):
                dve.wait_ge(hh_done, lin(item, 1, HT_NORMS + 1))
                dve.tensor_tensor(hflat_lo[:, 0:D].rearrange("p (a n) -> p a n", a=2), ps[:, 2:4, :],
                                  hflat_hi[:, 0:D].rearrange("p (a n) -> p a n", a=2), ALU.subtract).then_inc(ht_done, 1)

            def combine(r, t, bank=2):
                if t == 0:
                    dve.tensor_copy(gate_now, item_gate[:, :, bass.ds(r, 1)].rearrange("p t o -> p (t o)"))
                    dve.drain()
                dve.wait_ge(sc_done, r * TT + (t + 1))
                dve.scalar_tensor_tensor(two(x[:, t]), ps[:, bank:bank + 2, :], gate_now[:, t:t + 1],
                                         two(x[:, t]), ALU.mult, ALU.add).then_inc(comb_done, 1)

            one_hots(0)
            dve.wait_ge(expo_done, TT)
            dve.tensor_tensor(score, expo, sel, ALU.mult)
            dve.tensor_scalar(over, ps[:, 7, 2 * NE:3 * NE], P + 0.5, None, ALU.is_gt)
            dve.drain()
            dve.tensor_reduce(den, score, AX.X, ALU.add)
            dve.tensor_tensor(pair_gt[:, 0], over.unsqueeze(1).to_broadcast([P, NE, NE]), lower8, ALU.mult)
            dve.drain()
            dve.reciprocal(rden, den)
            dve.tensor_reduce(overpos, pair_gt[:, 0], AX.X, ALU.add)
            dve.drain()
            for t in range(TT):
                dve.tensor_scalar(item_gate[:, t, 1:1 + NE], score[:, t], rden[:, t:t + 1], None, ALU.mult)
            for k in range(3):
                dve.scalar_tensor_tensor(overhot[:, k], overpos, float(k), over, ALU.is_equal, ALU.mult)
            dve.drain()
            for what, to, at in ((item_pos[:, :, 0:NE], item_pos, NE), (item_gate[:, :, 1:1 + NE], item_gate, NE + 1)):
                for t in range(TT):
                    dve.tensor_tensor(scr8, overhot, what[:, t].unsqueeze(1).to_broadcast([P, 3, NE]), ALU.mult)
                    dve.drain()
                    dve.tensor_reduce(to[:, t, at:at + 3], scr8, AX.X, ALU.add)
                    dve.drain()
            dve.tensor_scalar(item_pos[:, :, NE:NE + 3], item_pos[:, :, NE:NE + 3], float(-P), None, ALU.add)
            dve.tensor_tensor(scr8, overhot, iota[:, 0:NE].unsqueeze(1).to_broadcast([P, 3, NE]), ALU.mult)
            dve.tensor_reduce(table[:, 0:1], over, AX.X, ALU.add)
            dve.drain()
            dve.tensor_reduce(table[:, 1:4], scr8, AX.X, ALU.add)
            dve.tensor_scalar(table[:, 0:1], table[:, 0:1], float(NE), None, ALU.add)
            dve.drain()
            dve.tensor_scalar(table[:, 1:4], table[:, 1:4], -1.0, 0.0, ALU.add, ALU.max)
            dve.drain()
            dve.tensor_copy(table_i[:, :], table).then_inc(tbl_done, 1)
            item_low(0)
            for y in (y_hi, y_lo):
                last = dve.tensor_scalar(y.rearrange("p (a n) -> p a n", n=P),
                                         ones[:, :].unsqueeze(1).to_broadcast([P, KT, P]), 0.0, None, ALU.mult)
            last.then_inc(yl_done, 1)
            split(U_MOE + 2)
            dve.wait_ge(tbl_done, 1)
            items = dve.value_load(table_i[0:1, 0:1], min_val=NE, max_val=MAX_ITEMS)
            with dve.Fori(0, items) as i:
                for n in range(3, ITEM_UNITS + 3):
                    kind, j, part = ITEM_ORDER[n - 3]
                    split(U_MOE + n, i, ITEM_UNITS, (0,))
                    if n == ITEM_UNITS + 2:
                        dve.wait_ge(yh_done, i + 1)
                        dve.tensor_tensor(two(y_lo), ps[:, 0:2, :], two(y_hi), ALU.subtract).then_inc(yl_done, 1)
                    if kind == "gu" and part == 1:
                        mult(ACT_FFN + j, 4 + j % 2, j % 2, rstd_slot, i, STEPS)
                    split(U_MOE + n, i, ITEM_UNITS, (1,))
                    done = tile_after(n - 3)
                    if done is not None:
                        act_low(ACT_FFN + done, 6 + done % 2, done % 2, i, STEPS)
                    if kind == "gu" and part == 0 and j - 1 in SCATTER_STEP:
                        combine(i, SCATTER_STEP.index(j - 1))
                    if kind == "gu" and part == 0 and j == ONEHOT_STEP + 1:
                        dve.wait_ge(onehT_ps, i + 1)
                        one_hots(i + 1)
                    if kind == "gu" and part == 1 and j == STEPS - 1:
                        item_low(i + 1)
            for t in range(TT):
                combine(items, t, 2 - 2 * t)
            dve.wait_ge(gf_in, 16)
            for t in range(TT):
                dve.wait_ge(std_done, 4 + t + 1)
                dve.reciprocal(rstd[:, 4, t:t + 1], std[:, 4, t:t + 1]).then_inc(rstd_done, 1)
                dve.wait_ge(rstd_done, 4 + t + 1)
                dve.scalar_tensor_tensor(x[:, t], x[:, t], rstd[:, 4, t:t + 1], xq[:, 0], ALU.mult,
                                         ALU.mult).then_inc(out_done, 1)

        @block.tensor
        def _(pe):
            def product(to, left, right, first, last):
                pe.matmul(to, left[0], right[0], start=first, stop=False, skip_group_check=True)
                pe.matmul(to, left[0], right[1], start=False, stop=False, skip_group_check=True)
                return pe.matmul(to, left[1], right[0], start=False, stop=last, skip_group_check=True)

            def half(at, reg=0, units=0):
                pe.wait_ge(lo_done, lin(reg, 2 * units, at + 1))
                return ring(at).start

            def weights(start, n):
                return whi[:, start:start + n], wlo[:, start:start + n]

            def to_cols(u, bank, reg=0, units=0, hs=(hT_hi, hT_lo), fresh=False):
                for h in range(2):
                    r0 = half(2 * u + h, reg, units)
                    if fresh:
                        pe.wait_ge(ht_done, 2 + 2 * h)
                    for c in range(2):
                        for k in range(4):
                            kt = 4 * h + k
                            last = product(ps[:, bank, c * SEQ:(c + 1) * SEQ].rearrange("p (t n) -> p t n", t=TT),
                                           weights(r0 + 256 * k + P * c, P),
                                           (hs[0][:, :, kt, :], hs[1][:, :, kt, :]),
                                           first=(h == 0 and c == 0 and k == 0), last=(kt == KT - 1))
                    last.then_inc(half_used, 1)

            def k_rows(u, kt0, left, tokens, banks, ends, reg=0, units=0, halves=(0, 1)):
                for h in halves:
                    r0 = half(2 * u + h, reg, units)
                    for t in range(tokens):
                        last = rows_product(r0, left(kt0 + h, t), banks[2 * t:2 * t + 2],
                                            ends[0] and h == 0, ends[1] and h == 1)
                    last.then_inc(half_used, 1)

            def rows_product(r0, left, banks, first, last):
                for c in range(2):
                    mm = product(ps[:, banks[c], :], left, weights(r0 + 512 * c, 512), first, last)
                return mm

            def k_rows_last(units, left, before_last):
                halves = [(2 * u + h, kt0 + h, first and h == 0) for u, kt0, first in units for h in range(2)]
                for t in range(TT):
                    for n, (at, kt, first) in enumerate(halves):
                        end = n == len(halves) - 1
                        if end and t == 1:
                            before_last()
                        last = rows_product(half(at), left(kt, t), (2 * t, 2 * t + 1), first, end)
                        if t == 1:
                            last.then_inc(half_used, 1)
                        elif end:
                            last.then_inc(y0_done, 1)

            def gate_up(ua, tokens, banks, reg=0, units=0, parts=(0, 1)):
                for part in parts:
                    for h in range(2):
                        r0 = half(2 * (ua + part) + h, reg, units)
                        for t in range(tokens):
                            for k in range(2):
                                kt = 4 * part + 2 * h + k
                                last = product(ps[:, banks[t], :], (hT_hi[:, t, kt, :], hT_lo[:, t, kt, :]),
                                               weights(r0 + 512 * k, 512), first=(kt == 0), last=(kt == KT - 1))
                        last.then_inc(half_used, 1)

            def mix_left(kt, t):
                return mixT_hi[:, kt, t * P:(t + 1) * P], mixT_lo[:, kt, t * P:(t + 1) * P]

            def h_left(kt, t):
                return hT_hi[:, t, kt, :], hT_lo[:, t, kt, :]

            def transpose_quarter(q):
                for k in range(4):
                    kt = 4 * (q % 2) + k
                    last = pe.transpose(ps[:, q, k * P:(k + 1) * P], x[:, q // 2, kt * P:(kt + 1) * P], ident[:, :])
                last.then_inc(tr_done, 1)

            def transposes(n, t):
                for q in (2 * t, 2 * t + 1):
                    pe.wait_ge(x_ready, 4 * (n - 1) + q + 1)
                    transpose_quarter(q)

            def spread_rstd(n):
                pe.wait_ge(diag_done, 2 * n)
                for t in range(TT):
                    last = pe.matmul(ps[:, 3, t * P:(t + 1) * P], ones[:, :], onehot[:, t, :], start=True, stop=True)
                last.then_inc(rrow_ps, 1)

            def act_transposes(n, bank, buf, reg=0, tiles=0):
                pe.wait_ge(act_done, lin(reg, tiles, n + 1))
                for s in range(2):
                    last = pe.transpose(ps[:, bank, s * P:(s + 1) * P], act_sb[:, buf, s * P:(s + 1) * P], ident[:, :])
                last.then_inc(at_done, 1)

            pe.wait_ge(ident_done, 1)
            pe.wait_ge(vec_in, 64)
            pe.transpose(ps[:, 7, 0:64], vrows, ident[0:64, 0:64]).then_inc(vecT_ps, 1)
            pe.wait_ge(x_in_s, 16 * TT)
            for q in FIRST_QUARTERS:
                transpose_quarter(q)

            def win_step(r, first):
                if not first:
                    pe.wait_ge(c_copied, r)
                to_cols(U_WIN, 4, r, 3, fresh=first)
                if first:
                    pe.wait_ge(const_done, 1)
                    spread_rstd(1)
                else:
                    pe.wait_ge(conv_done, r)
                to_cols(U_WIN + 1, 5, r, 3)
                to_cols(U_WIN + 2, 6, r, 3)

            win_step(0, True)
            with pe.Fori(1, 4) as r:
                win_step(r, False)
            for k in range(2):
                pe.wait_ge(cl_done, k + 1)
                k_rows(U_WOUT + k, 2 * k, mix_left, TT, range(4), (k == 0, False))
            pe.wait_ge(cl_done, 4)
            k_rows_last([(U_WOUT + 2, 4, False), (U_WOUT + 3, 6, False)], mix_left, lambda: transposes(1, 0))
            def act_left(h, t):
                return actT_hi[:, t, P * h:P * (h + 1)], actT_lo[:, t, P * h:P * (h + 1)]

            def down(u, r, ends, n, units=0):
                pe.wait_ge(al_done, lin(r, TT, n + TT))
                k_rows(u, 0, act_left, TT, range(4), ends, r, units)

            def ffn_step(r, ends):
                pe.wait_ge(act_done, lin(r, TT, TT))
                gate_up(U_FFN + 2, TT, (4, 5), r, 3)
                down(U_FFN + 4, r, ends, 0, 3)
                for b in range(TT):
                    act_transposes(TT + b, 6 + b, b, r, TT)

            for t in range(TT):
                for part in range(2):
                    for h in range(2):
                        r0 = half(2 * (U_FFN + part) + h)
                        if part + h == 0 and t == 0:
                            pe.wait_ge(ht_done, 4 + 1)
                        elif part == 1 and h == 0:
                            pe.wait_ge(ht_done, 4 + 2 * t + 2)
                        elif part + h == 0:
                            pe.wait_ge(ht_done, 4 + 2 * t + 1)
                        for k in range(2):
                            kt = 4 * part + 2 * h + k
                            last = product(ps[:, 4 + t, :], h_left(kt, t), weights(r0 + 512 * k, 512),
                                           first=(kt == 0), last=(kt == KT - 1))
                        if t == 1:
                            last.then_inc(half_used, 1)
                        elif part == 0 and h == 1:
                            transposes(1, 1)
            for b in range(TT):
                act_transposes(b, 6 + b, b)
            ffn_step(0, (True, False))
            with pe.Fori(1, STEPS - 2) as r:
                ffn_step(r, (False, False))
            pe.wait_ge(act_done, TT * (STEPS - 1))
            gate_up(U_V - 4, TT, (4, 5))
            pe.wait_ge(al_done, TT * (STEPS - 1))
            for t in range(TT):
                for h in range(2):
                    last = rows_product(half(2 * (U_V - 2) + h), act_left(h, t), (2 * t, 2 * t + 1), False, False)
                    if t == 1:
                        last.then_inc(half_used, 1)
                act_transposes(TT * (STEPS - 1) + t, 6 + t, t)

            def last_act_left(h, t):
                pe.wait_ge(al_done, TT * (STEPS - 1) + t + 1)
                return act_left(h, t)

            k_rows_last([(U_V - 1, 0, False)], last_act_left, lambda: transposes(2, 0))
            for t in range(TT):
                for u in range(3):
                    for h in range(2):
                        if (u, h) in ((0, 0), (2, 0)):
                            pe.wait_ge(ht_done, 8 + 2 * t + 1 + u // 2)
                        last = rows_product(half(2 * (U_V + u) + h), h_left(2 * u + h, t), (4 + 2 * t, 5 + 2 * t),
                                            u + h == 0, False)
                        if t == 1:
                            last.then_inc(half_used, 1)
                    if (t, u) == (0, 0):
                        transposes(2, 1)
            k_rows(U_V + 3, 6, h_left, TT, range(4, 8), (False, True))
            pe.wait_ge(hm_done, 16)
            for k in range(4):
                if k >= 2:
                    pe.wait_ge(kq_copied, k - 1)
                to_cols(U_K + k, k % 2)
                if k == 0:
                    spread_rstd(2)

            def queries(k):
                if k == 0:
                    pe.wait_ge(ht_done, 16)
                pe.wait_ge(kq_copied, 3 + k)
                to_cols(U_Q + k, k % 2, hs=(hq_hi, hq_lo))

            def scores(c):
                pe.wait_ge(kq_copied, 4 + c // 2 + 1)
                if c == 0:
                    pe.wait_ge(v_copied, 4)
                elif c == 2:
                    pe.wait_ge(rrow_done, 2)
                elif c > 2:
                    pe.wait_ge(o_copied, c - 2)
                for h in range(2):
                    rows = slice(HD * h, HD * (h + 1))
                    bank = Z_BANK[c] + h
                    pe.matmul(ps[:, bank, 0:SEQ], kT[rows, c, 0:P], qT[rows, c, 0:SEQ], start=True, stop=False,
                              skip_group_check=True)
                    pe.matmul(ps[:, bank, SEQ:SEQ + P], kT[rows, c, P:SEQ], qT[rows, c, P:SEQ], start=False,
                              stop=False, skip_group_check=True)
                    last = pe.matmul(ps[:, bank, :].rearrange("p (b n) -> p b n", b=4)[:, 0:4:2, :], ident_r,
                                     drop[:, :, :], start=False, stop=False, skip_group_check=True)
                last.then_inc(z_done, 1)

            def suffix_sums(c):
                pe.wait_ge(ll_done, c + 1)
                for h in range(2):
                    bank = Z_BANK[c] + h
                    for part in (l_hi[c % 2], l_lo[c % 2]):
                        pe.matmul(ps[:, bank, 0:384], neg_upto[:, :], part[:, h, :], start=False, stop=False,
                                  skip_group_check=True)
                        last = pe.matmul(ps[:, bank, P:SEQ], neg_all[:, :], part[:, h, SEQ:384], start=False, stop=True,
                                         skip_group_check=True)
                last.then_inc(s_done, 1)

            def weighted_values(c):
                pe.wait_ge(p_done, c + 1)
                for h in range(2):
                    rows = slice(HD * h, HD * (h + 1))
                    cols = slice((2 * c + h) * HD, (2 * c + h + 1) * HD)
                    pe.matmul(ps[rows, Z_BANK[c], 0:SEQ], vtok[:, 0, cols], wpart[c % 2][:, h, 0:SEQ], start=True,
                              stop=False, skip_group_check=True)
                    last = pe.matmul(ps[rows, Z_BANK[c], P:SEQ], vtok[:, 1, cols], wpart[c % 2][:, h, SEQ:384],
                                     start=False, stop=True, skip_group_check=True)
                last.then_inc(o_done, 1)

            def out_rows(k, halves):
                pe.wait_ge(ol_done, k + 1)
                k_rows(U_WO + k, 2 * k, mix_left, TT, range(4), (k == 0, False), halves=halves)

            def late_left(kt, t):
                pe.wait_ge(ol_done, kt // 2 + 1)
                return mix_left(kt, t)

            queries(0)
            queries(1)
            scores(0)
            scores(1)
            queries(2)
            for r in range(1, KT + 2):
                if r >= 2:
                    weighted_values(r - 2)
                if r <= KT:
                    suffix_sums(r - 1)
                if r + 1 < KT:
                    scores(r + 1)
                if r == 2:
                    queries(3)
                if r == 7:
                    pe.wait_ge(o_copied, 6)
                    out_rows(0, (0, 1))
                if r >= 8:
                    out_rows(1, (r - 8,))
            k_rows_last([(U_WO + 2, 4, False), (U_WO + 3, 6, False)], late_left, lambda: transposes(3, 0))
            transposes(3, 1)
            pe.wait_ge(rl_done, 1)
            for kt in range(KT):
                if kt % 4 == 0:
                    pe.wait_ge(ht_done, 16 + 3 + kt // 4)
                for n, (a, b) in enumerate(((rw_hi, hT_hi), (rw_hi, hT_lo), (rw_lo, hT_hi), (rw_lo, hT_lo))):
                    last = pe.matmul(ps[:, 6, 0:SEQ].rearrange("p (t n) -> p t n", t=TT), a[:, NE * kt:NE * kt + P],
                                     b[:, :, kt, :], start=(kt + n == 0), stop=(kt == KT - 1 and n == 3))
            last.then_inc(lT_ps, 1)
            pe.wait_ge(lT_done, 1)
            for t in range(TT):
                last = pe.transpose(ps[:, 7, NE * t:NE * (t + 1)], logitsT[:, t * P:(t + 1) * P], ident[0:NE, 0:NE])
            last.then_inc(logits_ps, 1)
            pe.wait_ge(sel_done, 1)
            pe.matmul(ps[:, 7, 0:NE], before[:, :], sel[:, 0], start=True, stop=True)
            pe.matmul(ps[:, 7, NE:2 * NE], ones[:, :], sel[:, 0], start=True, stop=False)
            pe.matmul(ps[:, 7, NE:2 * NE], before[:, :], sel[:, 1], start=False, stop=True)
            pe.matmul(ps[:, 7, 2 * NE:3 * NE], ones[:, :], sel[:, 0], start=True, stop=False)
            pe.matmul(ps[:, 7, 2 * NE:3 * NE], ones[:, :], sel[:, 1], start=False, stop=True).then_inc(pos_ps, 1)

            def gather(item):
                pe.wait_ge(oneh_done, item + 1)
                for q in range(2):
                    for n, (part, t) in enumerate(((xs_hi, 0), (xs_hi, 1), (xs_lo, 0), (xs_lo, 1))):
                        last = pe.matmul(ps[:, 2 + q, :], onehot_r[:, t, :], part[:, t, 512 * q:512 * (q + 1)],
                                         start=(n == 0), stop=(n == 3))
                    last.then_inc(xg_ps, 1)

            def gather_rstd():
                for t in range(TT):
                    last = pe.matmul(ps[:, 5, 0:1], onehot[:, t, :], rstd[:, 3, t:t + 1], start=(t == 0), stop=(t == 1))
                last.then_inc(rslot_ps, 1)

            def gather_transposes(item):
                for q in range(2):
                    pe.wait_ge(xg_done, item * 2 + (q + 1))
                    for k in range(4):
                        last = pe.transpose(ps[:, 2 + q, k * P:(k + 1) * P], hTf[:, q, k * P:(k + 1) * P], ident[:, :])
                    last.then_inc(tr_done, 1)

            def expert_down(j, i, halves=(0, 1)):
                pe.wait_ge(al_done, i * STEPS + (ACT_FFN + j + 1))
                k_rows(U_MOE + ITEM_ORDER.index(("down", j, 0)), 0,
                       lambda h, t: (actT_hi[:, j % 2, P * h:P * (h + 1)], actT_lo[:, j % 2, P * h:P * (h + 1)]),
                       1, (0, 1), (j == 0, j == STEPS - 1), i, ITEM_UNITS, halves)

            def scatter(r, t, bank=2):
                if t == 0:
                    pe.wait_ge(yl_done, r + 1)
                    pe.wait_ge(onehT_done, r + 1)
                elif bank == 2:
                    pe.wait_ge(comb_done, r * TT + 1)
                for c in range(2):
                    cols = slice(512 * c, 512 * c + 512)
                    pe.matmul(ps[:, bank + c, :], onehotT[:, t, :], y_hi[:, cols], start=True, stop=False)
                    last = pe.matmul(ps[:, bank + c, :], onehotT[:, t, :], y_lo[:, cols], start=False, stop=True)
                last.then_inc(sc_done, 1)

            pe.wait_ge(xs_done, TT)
            gather(0)
            gather_rstd()
            gather_transposes(0)
            pe.wait_ge(tbl_done, 1)
            items = pe.value_load(table_i[0:1, 0:1], min_val=NE, max_val=MAX_ITEMS)
            with pe.Fori(0, items) as i:
                pe.wait_ge(ht_done, i + (HT_NORMS + 1))
                for j in range(STEPS):
                    n = 0 if j == 0 else 3 * j - 1
                    pe.wait_ge(act_done, i * STEPS + (ACT_FFN + max(j - 1, 0)))
                    gate_up(U_MOE + n, 1, (4 + j % 2,), i, ITEM_UNITS, (0,))
                    if j == 1:
                        act_transposes(ACT_FFN, 6, 0, i, STEPS)
                    gate_up(U_MOE + n, 1, (4 + j % 2,), i, ITEM_UNITS, (1,))
                    if j in SCATTER_STEP:
                        scatter(i, SCATTER_STEP.index(j))
                    if j == ONEHOT_T_STEP:
                        pe.wait_ge(comb_done, i * TT + TT)
                        for t in range(TT):
                            last = pe.transpose(ps[:, 3, t * P:(t + 1) * P], onehot[:, t, :], ident[:, :])
                        last.then_inc(onehT_ps, 1)
                    if j == GATHER_STEP:
                        pe.wait_ge(onehT_done, i + 2)
                        gather(i + 1)
                    if j == GATHER_T_STEP:
                        gather_transposes(i + 1)
                    if j == STEPS - 1:
                        pe.wait_ge(act_done, i * STEPS + (ACT_FFN + j))
                        gather_rstd()
                        expert_down(j - 1, i, (0,))
                        act_transposes(ACT_FFN + j, 6 + j % 2, j % 2, i, STEPS)
                        expert_down(j - 1, i, (1,))
                    elif j > 0:
                        expert_down(j - 1, i)
                    if 0 < j < STEPS - 1:
                        act_transposes(ACT_FFN + j, 6 + j % 2, j % 2, i, STEPS)
                expert_down(STEPS - 1, i)
            for t in range(TT):
                scatter(items, t, 2 - 2 * t)


_INS = ["x", "g_mix", "g_ffn", "g_final", "a_w_in", "a_conv_w", "a_w_out", "g_kv", "w_kv", "b_w_q", "b_w_o",
        "ffn_w_gu", "ffn_w_down", "moe_w_router", "moe_w_gu", "moe_w_down"]


def kernel(**inputs):
    import numpy as np
    import concourse.bacc as bacc
    from concourse.bass_utils import run_bass_kernel_spmd

    nc = bacc.Bacc("TRN2", target_bir_lowering=False, num_devices=1)
    arrays, args = {}, []
    for name in _INS:
        a = np.ascontiguousarray(inputs[name])
        arrays[f"in_{name}"] = a
        args.append(nc.dram_tensor(f"in_{name}", a.shape, mybir.dt.from_np(a.dtype), kind="ExternalInput").ap())
    args.append(nc.dram_tensor("out_y", (1, SEQ, D), F32, kind="ExternalOutput").ap())
    trunk(nc, *args)
    r = run_bass_kernel_spmd(nc, [arrays], core_ids=[0])
    return r.results[0]["out_y"]
```
